# Optimizing a Trainium2 kernel written in Bass

```python
import math
import jax, jax.numpy as jnp
from jax import lax
import numpy as np

D_MODEL = 1024
BATCH = 1
SEQ = 512
DEPTH = 2

GRID_W = 64
CTX_LEN = 256
N_EVEN = (DEPTH + 1) // 2
N_ODD = DEPTH // 2
EPS = 1e-6

NA_HEADS = 8
NA_HEAD_DIM = 64
D_A = NA_HEADS * NA_HEAD_DIM
NA_WIN_H_MAX = 8
NA_WIN_W = 16
D_B = 512
CONV_WIDTH = 31
D_IN_AB = 3 * D_A + 2 * D_B
ML_HEADS = 8
ML_QK_DIM = 64
ML_V_DIM = 128
D_CQK = ML_HEADS * ML_QK_DIM
D_CV = ML_HEADS * ML_V_DIM
ML_SHORT_CONV = 5
ML_CHUNK = 128
D_IN_C = 2 * D_CQK + 2 * D_CV + 4 * ML_HEADS
ROPE_BASE = 10000.0
D_FF = ((math.ceil(8 * D_MODEL / 3) + 255) // 256) * 256

kernel_name = 'hybrid_na_conformer_mlstm_dit_block'

def rms_norm(x, g):
    xf = x.astype(jnp.float32)
    y = xf * lax.rsqrt(jnp.mean(xf * xf, axis=-1, keepdims=True) + EPS)
    return (y * g.astype(jnp.float32)).astype(x.dtype)

def layer_norm(x, g, b):
    xf = x.astype(jnp.float32)
    mu = jnp.mean(xf, axis=-1, keepdims=True)
    var = jnp.mean(jnp.square(xf - mu), axis=-1, keepdims=True)
    y = (xf - mu) * lax.rsqrt(var + EPS)
    return (y * g.astype(jnp.float32) + b.astype(jnp.float32)).astype(x.dtype)

def modulate(x, g, shift, scale):
    return rms_norm(x, g) * (1 + scale) + shift

def depthwise_conv(x, w, b):
    width = w.shape[0]
    pad = width // 2
    y = lax.conv_general_dilated(x, w[:, None, :].astype(x.dtype), window_strides=(1,),
                                 padding=[(pad, width - 1 - pad)],
                                 dimension_numbers=('NWC', 'WIO', 'NWC'),
                                 feature_group_count=x.shape[-1])
    return y + b

def rope_1d(xa, pos):
    nf = xa.shape[-1] // 2
    inv = ROPE_BASE ** (-jnp.arange(nf, dtype=jnp.float32) / nf)
    ang = pos.astype(jnp.float32)[:, None] * inv[None, :]
    cos = jnp.cos(ang)[None, :, None, :]
    sin = jnp.sin(ang)[None, :, None, :]
    x1 = xa[..., :nf].astype(jnp.float32)
    x2 = xa[..., nf:].astype(jnp.float32)
    return jnp.concatenate([x1 * cos - x2 * sin, x1 * sin + x2 * cos], axis=-1).astype(xa.dtype)

def axial_rope(x, row_pos, col_pos):
    half = x.shape[-1] // 2
    return jnp.concatenate([rope_1d(x[..., :half], row_pos), rope_1d(x[..., half:], col_pos)], axis=-1)

def swiglu(h, w_gate, w_up, w_down):
    return (jax.nn.silu(h @ w_gate) * (h @ w_up)) @ w_down

def neighbourhood_attention(q, k, v, k_ctx, v_ctx, rpb):
    B, T, H, dh = q.shape
    rows = T // GRID_W
    win_h = min(NA_WIN_H_MAX, rows)
    n_loc = win_h * NA_WIN_W
    qg = q.reshape(B, rows, GRID_W, H, dh)
    kg = k.reshape(B, rows, GRID_W, H, dh)
    vg = v.reshape(B, rows, GRID_W, H, dh)
    col = jnp.arange(GRID_W)
    c0 = jnp.clip(col - NA_WIN_W // 2, 0, GRID_W - NA_WIN_W)
    col_idx = c0[:, None] + jnp.arange(NA_WIN_W)[None, :]
    col_rel = col_idx - col[:, None] + (NA_WIN_W - 1)
    rpb_cols = rpb[:, :, col_rel]

    def row_block(r):
        r0 = jnp.clip(r - win_h // 2, 0, rows - win_h)
        q_r = lax.dynamic_index_in_dim(qg, r, axis=1, keepdims=False)
        k_rows = lax.dynamic_slice_in_dim(kg, r0, win_h, axis=1)
        v_rows = lax.dynamic_slice_in_dim(vg, r0, win_h, axis=1)
        k_win = k_rows[:, :, col_idx]
        v_win = v_rows[:, :, col_idx]
        s_loc = jnp.einsum('bchd,bacwhd->bhcaw', q_r, k_win).astype(jnp.float32)
        row_rel = r0 + jnp.arange(win_h) - r + (NA_WIN_H_MAX - 1)
        bias = jnp.take(rpb_cols, row_rel, axis=1).transpose(0, 2, 1, 3)
        s_loc = (s_loc + bias[None].astype(jnp.float32)).reshape(B, H, GRID_W, n_loc)
        s_ctx = jnp.einsum('bchd,bnhd->bhcn', q_r, k_ctx).astype(jnp.float32)
        p = jax.nn.softmax(jnp.concatenate([s_loc, s_ctx], axis=-1), axis=-1).astype(v.dtype)
        p_loc = p[..., :n_loc].reshape(B, H, GRID_W, win_h, NA_WIN_W)
        p_ctx = p[..., n_loc:]
        return (jnp.einsum('bhcaw,bacwhd->bchd', p_loc, v_win)
                + jnp.einsum('bhcn,bnhd->bchd', p_ctx, v_ctx))

    o = lax.map(row_block, jnp.arange(rows))
    return o.transpose(1, 0, 2, 3, 4).reshape(B, T, H * dh)

def na_conv_mixer(h_lat, h_ctx, w_in, q_g, k_g, rpb, conv_w, conv_b, ln_g, ln_b, w_out, ctx_out):
    def project(h):
        B, T, _ = h.shape
        q, k, v, u, gt = jnp.split(h @ w_in, [D_A, 2 * D_A, 3 * D_A, 3 * D_A + D_B], axis=-1)
        heads = lambda a: a.reshape(B, T, NA_HEADS, NA_HEAD_DIM)
        q = rms_norm(heads(q), q_g) * NA_HEAD_DIM ** -0.5
        k = rms_norm(heads(k), k_g)
        return q, k, heads(v), u * jax.nn.sigmoid(gt)

    def conv_module(glu):
        y = depthwise_conv(glu, conv_w, conv_b)
        return jax.nn.silu(layer_norm(y, ln_g, ln_b))

    qc, kc, vc, glu_c = project(h_ctx)
    ql, kl, vl, glu_l = project(h_lat)
    att_lat = neighbourhood_attention(ql, kl, vl, kc, vc, rpb)
    out_lat = jnp.concatenate([att_lat, conv_module(glu_l)], axis=-1) @ w_out
    out_ctx = None
    if ctx_out:
        B, N = qc.shape[:2]
        s = jnp.einsum('bnhd,bmhd->bhnm', qc, kc).astype(jnp.float32)
        p = jax.nn.softmax(s, axis=-1).astype(vc.dtype)
        att_c = jnp.einsum('bhnm,bmhd->bnhd', p, vc).reshape(B, N, D_A)
        out_ctx = jnp.concatenate([att_c, conv_module(glu_c)], axis=-1) @ w_out
    return out_lat, out_ctx

def mlstm_chunkwise(q, k, v, ig, lf, state, return_h):
    B, H, T, dk = q.shape
    L = min(ML_CHUNK, T)
    nc = T // L

    def chunks(a):
        a = a.astype(jnp.float32).reshape(a.shape[:2] + (nc, L) + a.shape[3:])
        return jnp.moveaxis(a, 2, 0)

    causal = jnp.tril(jnp.ones((L, L), dtype=bool))

    def step(carry, xs):
        S, n, m = carry
        qc, kc, vc, igc, lfc = xs
        b = jnp.cumsum(lfc, axis=-1)
        b_end = b[..., -1]
        w_end = b_end[..., None] - b + igc
        m_new = jnp.maximum(b_end + m, jnp.max(w_end, axis=-1))
        decay = jnp.exp(b_end + m - m_new)
        wk = jnp.exp(w_end - m_new[..., None])
        S_new = decay[..., None, None] * S + jnp.einsum('bhl,bhlk,bhlv->bhkv', wk, kc, vc)
        n_new = decay[..., None] * n + jnp.einsum('bhl,bhlk->bhk', wk, kc)
        if not return_h:
            return (S_new, n_new, m_new), None
        g = b + m[..., None]
        dmat = jnp.where(causal, b[..., :, None] - b[..., None, :] + igc[..., None, :], -jnp.inf)
        m_q = jnp.maximum(g, jnp.max(dmat, axis=-1))
        p = jnp.exp(dmat - m_q[..., None]) * jnp.einsum('bhik,bhjk->bhij', qc, kc)
        inter = jnp.exp(g - m_q)
        num = inter[..., None] * jnp.einsum('bhik,bhkv->bhiv', qc, S) + jnp.einsum('bhij,bhjv->bhiv', p, vc)
        den = inter * jnp.einsum('bhik,bhk->bhi', qc, n) + jnp.sum(p, axis=-1)
        h = num / jnp.maximum(jnp.abs(den), jnp.exp(-m_q))[..., None]
        return (S_new, n_new, m_new), h

    carry, h = lax.scan(step, state, (chunks(q), chunks(k), chunks(v), chunks(ig), chunks(lf)))
    if return_h:
        h = jnp.moveaxis(h, 0, 2).reshape(B, H, T, -1)
    return h, carry

def mlstm_mixer(h_lat, h_ctx, w_in, conv_w, conv_b, gate_b, norm_g, w_out, row_pos, col_pos, ctx_out):
    def project(h, use_rope):
        B, T, _ = h.shape
        qk, v, o, gates = jnp.split(h @ w_in, [2 * D_CQK, 2 * D_CQK + D_CV, 2 * D_CQK + 2 * D_CV], axis=-1)
        qk = jax.nn.silu(depthwise_conv(qk, conv_w, conv_b))
        q, k = jnp.split(qk, 2, axis=-1)
        q = q.reshape(B, T, ML_HEADS, ML_QK_DIM) * ML_QK_DIM ** -0.5
        k = k.reshape(B, T, ML_HEADS, ML_QK_DIM)
        if use_rope:
            q = axial_rope(q, row_pos, col_pos)
            k = axial_rope(k, row_pos, col_pos)
        v = v.reshape(B, T, ML_HEADS, ML_V_DIM)
        heads = lambda a: jnp.transpose(a, (0, 2, 1, 3))
        g = jnp.transpose(gates.astype(jnp.float32) + gate_b.astype(jnp.float32), (0, 2, 1))
        ig_f, ig_b, fg_f, fg_b = jnp.split(g, 4, axis=1)
        return (heads(q), heads(k), heads(v), o, ig_f, ig_b,
                jax.nn.log_sigmoid(fg_f), jax.nn.log_sigmoid(fg_b))

    rev = lambda a: jnp.flip(a, axis=2)
    qc, kc, vc, oc, igf_c, igb_c, lff_c, lfb_c = project(h_ctx, False)
    ql, kl, vl, ol, igf_l, igb_l, lff_l, lfb_l = project(h_lat, True)
    B, H = ql.shape[:2]
    zero = (jnp.zeros((B, H, ML_QK_DIM, ML_V_DIM), jnp.float32),
            jnp.zeros((B, H, ML_QK_DIM), jnp.float32),
            jnp.zeros((B, H), jnp.float32))
    hcf, st_f = mlstm_chunkwise(qc, kc, vc, igf_c, lff_c, zero, ctx_out)
    hcb, st_b = mlstm_chunkwise(rev(qc), rev(kc), rev(vc), rev(igb_c), rev(lfb_c), zero, ctx_out)
    hlf, _ = mlstm_chunkwise(ql, kl, vl, igf_l, lff_l, st_f, True)
    hlb, _ = mlstm_chunkwise(rev(ql), rev(kl), rev(vl), rev(igb_l), rev(lfb_l), st_b, True)

    def finish(h, o):
        Bh, Hh, T, dv = h.shape
        h = rms_norm(jnp.transpose(h, (0, 2, 1, 3)), norm_g.reshape(Hh, dv)).reshape(Bh, T, Hh * dv)
        return (h.astype(o.dtype) * jax.nn.sigmoid(o)) @ w_out

    out_lat = finish(hlf + rev(hlb), ol)
    out_ctx = finish(hcf + rev(hcb), oc) if ctx_out else None
    return out_lat, out_ctx

def setup_inputs(seed: int = 0) -> dict:
    key = jax.random.key(seed)
    ks = iter(jax.random.split(key, 40))
    nrm = lambda shape, s: jax.random.normal(next(ks), shape, jnp.float32) * s
    D = D_MODEL
    inp = {}
    inp['x'] = nrm((BATCH, SEQ, D), 1.0)
    inp['c'] = nrm((BATCH, D), 1.0)
    inp['ctx'] = nrm((BATCH, CTX_LEN, D), 1.0)
    inp['c_ctx'] = nrm((D,), 1.0)
    inp['ada_w'] = nrm((DEPTH, D, 6 * D), 0.5 * D ** -0.5)
    inp['ada_b'] = nrm((DEPTH, 6 * D), 0.02)
    inp['norm_mix_g'] = 1.0 + nrm((DEPTH, D), 0.02)
    inp['norm_ffn_g'] = 1.0 + nrm((DEPTH, D), 0.02)
    inp['ffn_w_gate'] = nrm((DEPTH, D, D_FF), D ** -0.5)
    inp['ffn_w_up'] = nrm((DEPTH, D, D_FF), D ** -0.5)
    inp['ffn_w_down'] = nrm((DEPTH, D_FF, D), D_FF ** -0.5)
    inp['ab_w_in'] = nrm((N_EVEN, D, D_IN_AB), D ** -0.5)
    inp['na_q_norm_g'] = 1.0 + nrm((N_EVEN, NA_HEAD_DIM), 0.02)
    inp['na_k_norm_g'] = 1.0 + nrm((N_EVEN, NA_HEAD_DIM), 0.02)
    inp['na_rpb'] = nrm((N_EVEN, NA_HEADS, 2 * NA_WIN_H_MAX - 1, 2 * NA_WIN_W - 1), 0.1)
    inp['conv_w'] = nrm((N_EVEN, CONV_WIDTH, D_B), CONV_WIDTH ** -0.5)
    inp['conv_b'] = nrm((N_EVEN, D_B), 0.02)
    inp['conv_ln_g'] = 1.0 + nrm((N_EVEN, D_B), 0.02)
    inp['conv_ln_b'] = nrm((N_EVEN, D_B), 0.02)
    inp['ab_w_out'] = nrm((N_EVEN, D_A + D_B, D), (D_A + D_B) ** -0.5)
    inp['ml_w_in'] = nrm((N_ODD, D, D_IN_C), D ** -0.5)
    inp['ml_conv_w'] = nrm((N_ODD, ML_SHORT_CONV, 2 * D_CQK), ML_SHORT_CONV ** -0.5)
    inp['ml_conv_b'] = nrm((N_ODD, 2 * D_CQK), 0.02)
    inp['ml_gate_b'] = jnp.concatenate([nrm((N_ODD, 2 * ML_HEADS), 0.1),
                                        3.0 + nrm((N_ODD, 2 * ML_HEADS), 0.5)], axis=-1)
    inp['ml_norm_g'] = 1.0 + nrm((N_ODD, D_CV), 0.02)
    inp['ml_w_out'] = nrm((N_ODD, D_CV, D), D_CV ** -0.5)
    return inp

def reference(x, c, ctx, c_ctx, ada_w, ada_b, norm_mix_g, norm_ffn_g, ffn_w_gate, ffn_w_up, ffn_w_down,
              ab_w_in, na_q_norm_g, na_k_norm_g, na_rpb, conv_w, conv_b, conv_ln_g, conv_ln_b, ab_w_out,
              ml_w_in, ml_conv_w, ml_conv_b, ml_gate_b, ml_norm_g, ml_w_out):
    T = x.shape[1]
    t = jnp.arange(T)
    row_pos = t // GRID_W
    col_pos = t % GRID_W
    s_lat = jax.nn.silu(c)
    s_ctx = jax.nn.silu(c_ctx)
    for l in range(DEPTH):
        last = l == DEPTH - 1
        j = l // 2
        mod_lat = (s_lat @ ada_w[l] + ada_b[l])[:, None, :]
        mod_ctx = s_ctx @ ada_w[l] + ada_b[l]
        sh1, sc1, g1, sh2, sc2, g2 = jnp.split(mod_lat, 6, axis=-1)
        csh1, csc1, cg1, csh2, csc2, cg2 = jnp.split(mod_ctx, 6, axis=-1)
        h_lat = modulate(x, norm_mix_g[l], sh1, sc1)
        h_ctx = modulate(ctx, norm_mix_g[l], csh1, csc1)
        if l % 2 == 0:
            out_lat, out_ctx = na_conv_mixer(h_lat, h_ctx, ab_w_in[j], na_q_norm_g[j], na_k_norm_g[j], na_rpb[j],
                                             conv_w[j], conv_b[j], conv_ln_g[j], conv_ln_b[j], ab_w_out[j],
                                             not last)
        else:
            out_lat, out_ctx = mlstm_mixer(h_lat, h_ctx, ml_w_in[j], ml_conv_w[j], ml_conv_b[j], ml_gate_b[j],
                                           ml_norm_g[j], ml_w_out[j], row_pos, col_pos, not last)
        x = x + g1 * out_lat
        x = x + g2 * swiglu(modulate(x, norm_ffn_g[l], sh2, sc2), ffn_w_gate[l], ffn_w_up[l], ffn_w_down[l])
        if not last:
            ctx = ctx + cg1 * out_ctx
            ctx = ctx + cg2 * swiglu(modulate(ctx, norm_ffn_g[l], csh2, csc2),
                                     ffn_w_gate[l], ffn_w_up[l], ffn_w_down[l])
    return x


_drawn_inputs = setup_inputs


def setup_inputs(seed=0):
    import zlib

    import numpy as np

    out = dict(_drawn_inputs(seed))
    spreads = {}
    factors = {'norm_mix_g': 8.0,
     'norm_ffn_g': 6.523,
     'na_q_norm_g': 8.0,
     'na_k_norm_g': 8.0,
     'na_rpb': 8.0,
     'conv_b': 8.0,
     'conv_ln_g': 24.254,
     'conv_ln_b': 25.829,
     'ml_conv_b': 64.0,
     'ml_norm_g': 64.0}
    for name, (base, spread) in spreads.items():
        noise = np.random.default_rng([zlib.crc32(name.encode()), seed]).standard_normal(out[name].shape)
        drawn = base * np.exp(spread * noise) if base else spread * noise
        out[name] = __import__('jax').numpy.asarray(drawn.astype(out[name].dtype))
    for name, factor in factors.items():
        out[name] = (out[name] * factor).astype(out[name].dtype)
    return out
```

```python
import concourse.bass as bass
from concourse import mybir
from contextlib import ExitStack
import numpy as np

D = 1024
KT = D // 128
LAT, CTX = 512, 256
T = LAT + CTX
F = 2816
FT = F // 128
GD_END = 59
GROUPS = ((0, 8), (8, 8), (16, 6))
GRID = 64
ROWS = LAT // GRID
WIN = 16
TAPS = 31
MTAPS = 5
EPS = 1e-6
BIG = 1e30
CH = LAT // 128
NC = T // 128

R_V = 0
R_AB = R_V + 4
R_O0 = R_AB + 16
R_F0 = R_O0 + 8
R_ML = R_F0 + 2 * FT + 24
R_GATE = R_ML + 16
R_O1 = R_GATE + 8
R_F1 = R_O1 + 8
NR = R_F1 + 2 * FT + 24

SM = {}
_at = 0
for _name, _n in (("ada_b", 96), ("mix_g", 16), ("ffn_g", 16), ("q_g", 1), ("k_g", 1), ("conv_w", 4 * TAPS),
                  ("conv_b", 4), ("ln_g", 4), ("ln_b", 4), ("mconv_w", 8 * MTAPS), ("mconv_b", 8),
                  ("mnorm_g", 8), ("c", 16)):
    SM[_name] = (_at, _at + _n)
    _at += _n
NSM = _at
CN = {}
_at = 0
for _name, _n in (("ident", 128), ("flip", 128), ("upto", 128), ("from", 128), ("pair", 128), ("ones", 128),
                  ("rot", 128), ("cos", LAT), ("sin", LAT)):
    CN[_name] = (_at, _at + _n)
    _at += _n
NCN = _at

KB_OFF = (0, 64, 192, 320, 448)
VSLOT = {1: 0, 2: 1, 3: 2, 5: 3, 6: 4, 0: 5, 4: 6}
VPIECES = ((1, 64, 128), (2, 192, 128), (3, 320, 128), (5, 512, 128), (6, 640, 128), (0, 0, 64), (4, 448, 64))


def key_blocks(t):
    out = [(5, 0, 128), (6, 128, 128)]
    if t < 4:
        n0 = 64 if t == 0 else 128
        n1 = 64 if t == 3 else 128
        out += sorted([(t, 256, n0), (t + 1, 256 + n0, n1)], key=lambda b: -b[2])
    return out


def program(nc, A, out):
    f32, f32r = mybir.dt.float32, mybir.dt.float32r
    ACT, ALU, AX = mybir.ActivationFunctionType, mybir.AluOpType, mybir.AxisListType
    ctx = ExitStack()
    with ctx:
        def sb(name, shape, dt=f32):
            return ctx.enter_context(nc.sbuf_tensor(name, shape, dt))

        def sem(name):
            return ctx.enter_context(nc.semaphore(name))

        X = sb("X", [128, KT, T])
        h_hi, h_lo = sb("h_hi", [128, KT, T], f32r), sb("h_lo", [128, KT, T], f32r)
        c_hi, c_lo = sb("c_hi", [128, KT, T], f32r), sb("c_lo", [128, KT, T], f32r)
        raw = sb("raw", [128, 2, 1024])
        w_hi, w_lo = sb("w_hi", [128, 2, KT, 128], f32r), sb("w_lo", [128, 2, KT, 128], f32r)
        adaw = sb("adaw", [128, 2, 1024])
        small = sb("small", [128, NSM])
        const = sb("const", [128, NCN])
        mod = sb("mod", [128, 96, 2])
        amod = sb("amod", [128, 4, KT, 2])
        sT = sb("sT", [128, KT, 2])
        NSCR = 11000
        scr = sb("scr", [128, NSCR])
        PS = ctx.enter_context(nc.psum_tensor("PS", [128, 8, 512], f32))
        PSf = PS[:, :, :].rearrange("p b n -> p (b n)")
        G = [PSf[:, 0:1024], PSf[:, 1024:2048]]
        x_spill = nc.dram_tensor("x_spill", (128, KT, LAT), f32, kind="Internal").ap()

        def cn(name):
            return const[:, CN[name][0]:CN[name][1]]

        def sm(name, i, n=1):
            return small[:, SM[name][0] + i:SM[name][0] + i + n]

        ident, flip, ones = cn("ident"), cn("flip"), cn("ones")
        Xf = X[:, :, :].rearrange("p k t -> p (k t)")

        def carve(base, at, *shape):
            n = int(np.prod(shape))
            v = base[:, at:at + n]
            if len(shape) == 2:
                v = v.rearrange("p (a b) -> p a b", a=shape[0])
            if len(shape) == 3:
                v = v.rearrange("p (a b c) -> p a b c", a=shape[0], b=shape[1])
            if len(shape) == 4:
                v = v.rearrange("p (a b c d) -> p a b c d", a=shape[0], b=shape[1], c=shape[2])
            return v, at + n

        nt, at = carve(scr, 0, 2, T)
        nt2, at = carve(scr, at, 2, T)
        nrs, at = carve(scr, at, T)
        sg, at = carve(scr, 0, T)
        ftmp, at = carve(scr, at, T)
        convy, at = carve(Xf, 0, 4, LAT + CTX + 30)
        glu, at = carve(Xf, at, LAT + CTX + 60)
        braw, at = carve(Xf, at, ROWS, 8, 32)
        assert at <= KT * T
        Vt, at = carve(scr, 0, 7, 512)
        bx, at = carve(scr, at, 448 + 512 + 448)
        qB, at = carve(scr, at, T)
        kB, at = carve(scr, at, T)
        Pb, at = carve(scr, at, 2, 512)
        PTs, at = carve(scr, at, 2, 512)
        sqb, _ = carve(scr, at - 2048, 2, T)
        rsb, at = carve(scr, at, 2, T)
        sgm, at = carve(scr, at, T)
        atmp, at = carve(scr, at, 16)
        assert at <= NSCR, at
        vT = sgm
        BX = (0, 448, 960)
        lnt, lnm = sqb, rsb
        hsum, at = carve(Xf, 0, CH, 8, 128)
        kw, at = carve(Xf, at, 2, NC, 128)
        assert at <= KT * T
        vaug, at = carve(scr, 0, 2, NC, 129)
        qpad, at = carve(scr, at, LAT + 4)
        kpad, at = carve(scr, at, LAT + CTX + 8)
        ks, at = carve(scr, at, LAT + 4 + CTX)
        qr, at = carve(scr, at, LAT)
        kr, at = carve(scr, at, LAT)
        mt, at = carve(scr, at, LAT)
        Sst, at = carve(scr, at, 2, 6, 129)
        Eb, at = carve(scr, at, LAT)
        qs, _ = carve(scr, at, LAT)
        Pm, at = carve(scr, at, 2, LAT)
        vt1, _ = carve(scr, at, T)
        qi, at = carve(scr, at, 2, LAT)
        kqm, at = carve(scr, at, LAT)
        ib, at = carve(scr, at, LAT)
        rsel, at = carve(scr, at, LAT)
        nga, at = carve(scr, at, 96)
        assert at <= NSCR, at
        adf = adaw[:, :, :].rearrange("p a n -> p (a n)")
        gall, at = carve(adf, 0, NC, 32)
        lf, at = carve(adf, at, 2, NC, 8)
        bb, at = carve(adf, at, 2, 96)
        ga, at = carve(adf, at, 96)
        gM, at = carve(adf, at, 96)
        gcm, at = carve(adf, at, 2, 48)
        mB, at = carve(adf, at, 96)
        mA, at = carve(adf, at, 96)
        ge, at = carve(adf, at, 3, 96)
        rcol, at = carve(adf, at, 96)
        arow, at = carve(adf, at, 2, 128)
        cmrow, at = carve(adf, at, 2, 128)
        mx48, at = carve(adf, at, 2)
        dM, at = carve(adf, at, 2, 48)
        dcomb, at = carve(adf, at, 2, 6)
        den, at = carve(adf, at, 2, CH)
        ssq, at = carve(adf, at, 2, CH)
        gb, at = carve(adf, at, 32)
        assert at <= 2048, at
        nrow = arow
        eps, qg8 = sb("eps", [128, 1]), sb("qg8", [128, 1])
        wg_raw = Eb[:, 0:256]
        wg_hi, wg_lo = sb("wg_hi", [128, KT, 32], f32r), sb("wg_lo", [128, KT, 32], f32r)

        s_raw = [sem("raw0_loaded"), sem("raw1_loaded")]
        s_hi, s_lo, s_gemm = sem("w_hi_ready"), sem("w_lo_ready"), sem("product_done")
        s_gf = [sem("psum0_free"), sem("psum1_free")]
        s_small, s_x, s_const = sem("small_loaded"), sem("x_loaded"), sem("const_loaded")
        s_ada0 = [sem(f"ada_first{i}_loaded") for i in range(4)]
        s_adl = [sem("ada0_loaded"), sem("ada1_loaded")]
        s_sT, s_adm, s_mod, s_amod = sem("cond_ready"), sem("ada_product_done"), sem("mod_ready"), sem("amod_ready")
        s_nsq, s_nss, s_nrs = sem("norm_square_ready"), sem("norm_sum_done"), sem("norm_rstd_ready")
        s_nln, s_nt, s_naf = sem("norm_log_ready"), sem("norm_scaled_ready"), sem("norm_affine_ready")
        s_nhi, s_h = sem("norm_hi_ready"), sem("h_ready")
        s_hhi, s_hid = sem("hidden_hi_ready"), sem("hidden_ready")
        s_braw, s_vX, s_v = sem("bias_loaded"), sem("v_transposed"), sem("v_ready")
        s_zero, s_bx, s_pool = sem("zeroed"), sem("bias_masked"), sem("pool_step")
        s_sq, s_ss, s_ln, s_rs = sem("qk_square"), sem("qk_sum"), sem("qk_log"), sem("qk_rstd")
        s_S, s_neg, s_E, s_Pn = sem("scores_ready"), sem("neg_max_ready"), sem("exp_ready"), sem("probs_ready")
        s_mx = sem("max_ready")
        s_Tr, s_PT, s_O, s_ahi, s_alo = (sem("probs_transposed"), sem("probsT_ready"), sem("attn_done"),
                                         sem("attn_hi_ready"), sem("attn_lo_ready"))
        s_conv = sem("conv_step")
        s_lns, s_lnp, s_lna, s_lnd, s_cat = sem("ln_stat_done"), sem("ln_act"), sem("ln_rstd"), sem("ln_step"), sem("cat_ready")
        s_q8, s_eps, s_xpart = sem("gain_scaled"), sem("eps_set"), sem("x_latent_updated")
        s_rel = sem('relu_done')
        s_PTa, s_rr = sem("probsT_full_ready"), sem("rsum_inverse")
        s_spill, s_back = sem("x_spilled"), sem("x_back")
        s_gw, s_wgh, s_wgl, s_g1, s_g2 = sem("gatew_loaded"), sem("gatew_hi"), sem("gatew_lo"), sem("gate_pe"), sem("gate_dve")
        s_g3 = sem("gate_act")
        s_pad, s_mcv, s_sil, s_rot, s_rope = sem("padded"), sem("mconv_step"), sem("silu_ready"), sem("rot_done"), sem("rope_step")
        s_kT, s_kw, s_vt1, s_vtp, s_va = sem("k_transposed"), sem("kw_ready"), sem("vt_ready"), sem("vt_transposed"), sem("vaug_ready")
        s_su, s_st = sem("update_done"), sem("state_step")
        s_kq, s_rs2, s_R, s_E2, s_ib, s_qi = (sem("kq_done"), sem("rsel_ready"), sem("R_done"), sem("E_ready"),
                                              sem("inter_ready"), sem("qi_ready"))
        s_km, s_Pm, s_num, s_den, s_hs, s_ha = (sem("kqm_ready"), sem("pm_ready"), sem("num_done"), sem("den_step"),
                                                sem("head_out"), sem("head_sum"))
        s_rn, s_rna, s_hn = sem("rms_act"), sem("rms_dve"), sem("head_normed")
        s_hT, s_og, s_otmp, s_ohi, s_ocat = (sem("headT_done"), sem("o_sigmoid"), sem("o_tmp"), sem("o_hi"), sem("ocat_ready"))
        s_out = sem("out_stored")
        block = ctx.enter_context(nc.Block())

        NORM_T = (T, T, T, LAT)

        def norm_cols(w):
            return ((0, 0, LAT), (1, LAT, T)) if NORM_T[w] == T else ((0, 0, LAT),)

        @block.sync
        def _(sp):
            sp.dma_start(small[:], A["small"]).then_inc(s_small, 16)
            scr_w = scr[:, 0:8192].rearrange("p (a n) -> p a n", a=8)
            for i in range(2):
                sp.dma_start(scr_w[:, 4 * i:4 * i + 4], A["ada"][4 * i:4 * i + 4].rearrange("a p n -> p a n"))\
                  .then_inc(s_ada0[i], 16)
            sp.dma_start(X[:], A["xT"]).then_inc(s_x, 16)
            sp.dma_start(const[:], A["const"]).then_inc(s_const, 16)
            for i in range(2, 4):
                sp.wait_ge(s_adm, 4 * (i - 1))
                sp.dma_start(scr_w[:, 4 * i - 8:4 * i - 4], A["ada"][4 * i:4 * i + 4].rearrange("a p n -> p a n"))\
                  .then_inc(s_ada0[i], 16)
            for r in range(2):
                sp.dma_start(raw[:, r], A["w"][r]).then_inc(s_raw[r], 16)
            with sp.Fori(1, NR // 2) as i:
                r = sp.snap(2 * i)
                for j in range(2):
                    src = A["w"][bass.ds(sp.snap(r + j), 1)].rearrange("a p n -> p (a n)")
                    sp.wait_ge(s_lo, r + (j - 1))
                    sp.dma_start(raw[:, j], src).then_inc(s_raw[j], 16)

        @block.gpsimd
        def _(pool):
            pool.wait_ge(s_h, 8)
            for v in (glu[:], bx[:]):
                nc.gpsimd.memset(v, 0.0).then_inc(s_zero, 1)
            for c in range(16):
                src = bass.AP(A["rpb"].tensor, 7 * 384 + 7 * 48 + 15 - c, [[384, 8], [-48, 64], [1, 32]])
                pool.dma_start(braw[8 * c:8 * c + 8].rearrange("p a h k -> p (a h) k"), src).then_inc(s_braw, 16)
            pool.wait_ge(s_braw, 256)
            pool.wait_ge(s_zero, 2)
            for H in range(8):
                if H:
                    pool.wait_ge(s_mx, 4 * H)
                for kind, first, k0, k1, kb0, kn, keep in (
                        (0, 256, 8, 16, 8, 8, "low"), (0, 320, 16, 24, 16, 16, None), (0, 320, 24, 32, 16, 16, "high"),
                        (1, 256, 0, 16, 0, 16, "low"), (1, 384, 16, 32, 16, 16, "high"),
                        (2, 256, 0, 8, 0, 16, "low"), (2, 256, 8, 16, 0, 16, None), (2, 384, 16, 24, 16, 8, "high")):
                    dst = bx[:, BX[kind] + first:BX[kind] + first + 8 * kn].rearrange("p (a k) -> p a k", a=8)
                    dst = dst[:, :, k0 - kb0:k1 - kb0]
                    src = braw[:, :, H, k0:k1]
                    if keep is None:
                        i = nc.gpsimd.tensor_copy(dst, src)
                    elif keep == "low":
                        i = nc.gpsimd.affine_select(out=dst, in_=src, compare_op=ALU.is_ge, fill=-BIG, base=8 * k0 + 7,
                                                    pattern=[[0, 8], [8, k1 - k0]], channel_multiplier=-1)
                    else:
                        i = nc.gpsimd.affine_select(out=dst, in_=src, compare_op=ALU.is_ge, fill=-BIG, base=120 - 8 * k0,
                                                    pattern=[[0, 8], [-8, k1 - k0]], channel_multiplier=1)
                    i.then_inc(s_bx, 1)
            pool.wait_ge(s_g2, GD_END)
            for n in range(16):
                H, d = n // 2, n % 2
                if n:
                    pool.wait_ge(s_R, n)
                row = nrow[0:48, d, None, :].to_broadcast([48, CH, 128])
                pick = ident[0:48, H:32:8][:, :, None].to_broadcast([48, CH, 128])
                nc.gpsimd.tensor_tensor(rsel[0:48].rearrange("p (c i) -> p c i", c=CH), row, pick, ALU.mult)\
                    .then_inc(s_rs2, 1)

        def split_hi(act, half, j, first=False):
            act.wait_ge(s_raw[j], 16 * half + 16)
            if not first:
                act.wait_ge(s_gemm, 2 * half + (j - 1))
            nc.scalar.activation(w_hi[:, j], raw[:, j].rearrange("p (k n) -> p k n", k=KT), ACT.Copy).then_inc(s_hi, 1)

        def split_lo(dve, half, j):
            dve.wait_ge(s_hi, 2 * half + (j + 1))
            nc.vector.tensor_tensor(w_lo[:, j], raw[:, j].rearrange("p (k n) -> p k n", k=KT),
                                    w_hi[:, j].bitcast(f32), ALU.subtract).then_inc(s_lo, 1)

        def product(pe, half, j, m_hi, m_lo, cols, k_tiles=KT, first=False):
            pe.wait_ge(s_lo, 2 * half + (j + 1))
            if not first:
                pe.wait_ge(s_gf[j], half)
            n = 0
            for k in range(k_tiles):
                for w, m in ((w_hi, m_hi), (w_hi, m_lo), (w_lo, m_hi)):
                    n += 1
                    for a, b in cols:
                        last = nc.tensor.matmul(G[j][:, a:b], w[:, j, k], m[:, k, a:b],
                                                start=(n == 1), stop=(n == 3 * k_tiles))
            last.then_inc(s_gemm, 1)

        BOTH = ((0, LAT), (LAT, T))
        ONLY = ((0, LAT),)
        SSA = PSf[:, 2048:2048 + T]
        SSB = PSf[:, 3072:3072 + T]
        ADP = PSf[:, 7 * 512 + 256:7 * 512 + 512]
        ADM = PSf[:, 512:528]
        PB, OB = (6, 2), (7, 3)
        ADQ = PSf[:, 4 * 512:4 * 512 + 8]
        LAY_COLS = (BOTH, ONLY)

        SH1, SC1, G1, SH2, SC2, G2 = (8 * i for i in range(6))
        NORM_SH = (SH1, SH2, 48 + SH1, 48 + SH2)
        NORM_SC = (SC1, SC2, 48 + SC1, 48 + SC2)
        MOD_N = (1, 5, 17, 17)
        XUP = {1: R_O0 + 8, 2: R_ML, 3: R_O1 + 8}

        def attn_hi(act, hp, u):
            h, t, U = u // 6, u % 6, 12 * hp + u
            act.wait_ge(s_O, U + 1)
            dst, src = attn_views(c_hi, hp, h, t, U)
            nc.scalar.activation(dst, src, ACT.Copy).then_inc(s_ahi, 1)

        def attn_views(c, hp, h, t, U):
            hr = slice(64 * h, 64 * h + 64)
            src = PS[hr, OB[U % 2], 0:128]
            if t < 4:
                dst = c[hr, hp, 0:LAT].rearrange("p (r t c) -> p t c r", r=ROWS, t=4)[:, t]
                return dst, src.rearrange("p (c r) -> p c r", c=16)
            return c[hr, hp, LAT + 128 * (t - 4):LAT + 128 * (t - 3)], src

        def transpose_v(pe, i):
            if i:
                pe.wait_ge(s_v, 2 * i)
            pe.wait_ge(s_gf[i % 2], i // 2 + 1)
            for b, c, size in VPIECES:
                s = VSLOT[b]
                last = nc.tensor.transpose(PSf[0:size, 2048 + 128 * s:2176 + 128 * s], vT[:, c:c + size], ident)
            last.then_inc(s_vX, 1)

        @block.scalar
        def _(act):
            def ada_load(a):
                if a >= 18:
                    act.wait_ge(s_adm, a - 1)
                act.dma_start(adaw[:, a % 2], A["ada"][a]).then_inc(s_adl[a % 2], 16)

            def norm(w):
                cols = NORM_T[w]
                if w == 0:
                    act.wait_ge(s_x, 16)
                else:
                    for j in range(2):
                        act.wait_ge(s_gf[j], XUP[w] // 2)
                for k in range(KT):
                    n = 8 * w + k
                    if k >= 2:
                        act.wait_ge(s_nss, n - 1)
                    nc.scalar.activation(nt[:, k % 2, 0:cols], X[:, k, 0:cols], ACT.Square).then_inc(s_nsq, 1)
                act.wait_ge(s_nss, 8 * w + 8)
                nc.scalar.activation(nrs[:, 0:cols], SSA[:, 0:cols], ACT.Ln, scale=1.0 / D, bias=eps[:]).then_inc(s_nln, 1)
                act.wait_ge(s_nln, w + 1)
                nc.scalar.activation(nrs[:, 0:cols], nrs[:, 0:cols], ACT.Exp, scale=-0.5).then_inc(s_nrs, 1)
                act.wait_ge(s_amod, (1, 2, 4, 4)[w])
                na = 16 * w
                for k in range(KT):
                    n = 8 * w + k
                    act.wait_ge(s_nt, n + 1)
                    if k >= 2:
                        act.wait_ge(s_h, n - 1)
                    for s, a, b in norm_cols(w):
                        nc.scalar.activation(nt2[:, k % 2, a:b], nt[:, k % 2, a:b], ACT.Identity,
                                             scale=amod[:, w, k, s:s + 1],
                                             bias=mod[:, NORM_SH[w] + k, s:s + 1]).then_inc(s_naf, 1)
                        na += 1
                    act.wait_ge(s_naf, na)
                    nc.scalar.activation(h_hi[:, k, 0:cols], nt2[:, k % 2, 0:cols], ACT.Copy).then_inc(s_nhi, 1)

            def ffn(layer):
                cols = NORM_T[2 * layer]  if layer == 0 else LAT
                R = R_F0 if layer == 0 else R_F1
                for g, (f0, nf) in enumerate(GROUPS):
                    with act.Fori(0, nf) as i:
                        half = act.snap(i + R // 2)
                        n = act.snap(i + layer * FT + f0)
                        split_hi(act, half, 1)
                        act.wait_ge(s_gemm, 2 * half + 1)
                        act.wait_ge(s_gf[1], half)
                        nc.scalar.activation(sg[:, 0:cols], G[0][:, 0:cols], ACT.Silu).then_inc(s_gf[0], 1)
                        split_hi(act, half + 1, 0)
                        act.wait_ge(s_gf[1], half + 1)
                        nc.scalar.activation(c_hi[:, bass.ds(i, 1), 0:cols].rearrange("p a n -> p (a n)"),
                                             ftmp[:, 0:cols], ACT.Copy).then_inc(s_hhi, 1)
                    R += 2 * nf
                    last = 1 if (layer == 1 and g == 2) else 0
                    with act.Fori(0, 4 - last) as i:
                        half = act.snap(i + R // 2)
                        na = act.snap(4 * i + (48 + 16 * g))
                        split_hi(act, half, 1)
                        if layer == 0:
                            for q in range(2):
                                src = A["ada"][bass.ds(act.snap(na + q), 1)].rearrange("a p n -> p (a n)")
                                act.wait_ge(s_adm, na + (q - 1))
                                act.dma_start(adaw[:, q], src).then_inc(s_adl[q], 16)
                        split_hi(act, half + 1, 0)
                        if layer == 0:
                            for q in range(2, 4):
                                src = A["ada"][bass.ds(act.snap(na + q), 1)].rearrange("a p n -> p (a n)")
                                act.wait_ge(s_adm, na + (q - 1))
                                act.dma_start(adaw[:, q - 2], src).then_inc(s_adl[q - 2], 16)
                    if last:
                        split_hi(act, (NR - 2) // 2, 1)
                    R += 8

            def out_proj(layer):
                R = R_O0 if layer == 0 else R_O1
                with act.Fori(0, 4) as i:
                    half = act.snap(i + R // 2)
                    split_hi(act, half, 1)
                    split_hi(act, half + 1, 0)

            act.wait_ge(s_small, 16)
            nc.scalar.activation(sT[:].rearrange("p k s -> p (k s)"), sm("c", 0, 16), ACT.Silu).then_inc(s_sT, 1)
            act.wait_ge(s_adm, 16)
            act.wait_ge(s_eps, 1)
            norm(0)
            split_hi(act, 0, 0, first=True)
            for i in range(4):
                half, j = (R_V + i) // 2, i % 2
                split_hi(act, (i + 1) // 2, (i + 1) % 2, first=(i == 0))
                act.wait_ge(s_gemm, i + 1)
                if i:
                    act.wait_ge(s_vX, i)
                g = G[j]
                gr = g[:, 0:LAT].rearrange("p (a c) -> p a c", a=ROWS)
                nc.scalar.activation(vT[:, 0:64].rearrange("p (a c) -> p a c", a=8), gr[:, :, 0:8], ACT.Copy)
                for b in range(3):
                    nc.scalar.activation(vT[:, 64 + 128 * b:192 + 128 * b].rearrange("p (a c) -> p a c", a=8),
                                         gr[:, :, 8 + 16 * b:24 + 16 * b], ACT.Copy)
                nc.scalar.activation(vT[:, 448:512].rearrange("p (a c) -> p a c", a=8), gr[:, :, 56:64], ACT.Copy)
                nc.scalar.activation(vT[:, LAT:T], g[:, LAT:T], ACT.Copy).then_inc(s_gf[j], 1)
            for hp in range(4):
                r = R_AB + 4 * hp
                half = r // 2
                split_hi(act, half, 1)
                for x in range(2):
                    act.wait_ge(s_gemm, r + x + 1)
                    if hp:
                        act.wait_ge(s_ss, 2 * hp)
                    nc.scalar.activation(sqb[:, x], G[x][:, 0:T], ACT.Square).then_inc(s_sq, 1)
                    split_hi(act, half + 1, x)
                for x in range(2):
                    act.wait_ge(s_ss, 2 * hp + x + 1)
                    nc.scalar.activation(rsb[:, x], (SSA, SSB)[x], ACT.Ln, scale=1.0 / 64, bias=eps[:]).then_inc(s_ln, 1)
                    act.wait_ge(s_ln, 2 * hp + x + 1)
                    nc.scalar.activation(rsb[:, x], rsb[:, x], ACT.Exp, scale=-0.5).then_inc(s_rs, 1)
                act.wait_ge(s_gemm, r + 4)
                if hp:
                    act.wait_ge(s_gf[0], half)
                else:
                    act.wait_ge(s_vX, 4)
                nc.scalar.activation(sgm[:], G[1][:, 0:T], ACT.Sigmoid).then_inc(s_gf[1], 1)
                split_hi(act, half + 2, 0)
                for u in range(12):
                    h, t, U = u // 6, u % 6, 12 * hp + u
                    a = 16 + 8 * hp + u
                    if u < 8:
                        ada_load(a)
                    act.wait_ge(s_neg, U + 1)
                    nk = 256 + sum(b[2] for b in key_blocks(t)[2:])
                    src = Pb[:, U % 2, 0:nk] if t < 4 else PS[:, 4 + U % 2, 0:256]
                    if t >= 4 and U >= 2:
                        act.wait_ge(s_Tr, U - 1)
                    nc.scalar.activation(Pb[:, U % 2, 0:nk], src, ACT.Exp, bias=atmp[:, 2 + U % 2:3 + U % 2],
                                         accum_out=atmp[:, 4 + U % 2:5 + U % 2]).then_inc(s_E, 1)
                    if u:
                        attn_hi(act, hp, u - 1)
                    act.wait_ge(s_Tr, U + 1)
                    if U >= 2:
                        act.wait_ge(s_O, U - 1)
                    blocks = key_blocks(t)
                    full = sum(1 for b in blocks if b[2] == 128)
                    n = nc.scalar.activation(PTs[:, U % 2, 0:128 * full], PS[:, PB[U % 2], 0:128 * full], ACT.Copy)
                    if full < len(blocks):
                        n.then_inc(s_PTa, 1)
                        n = nc.scalar.activation(PTs[0:64, U % 2, 384:512], PS[0:64, PB[U % 2], 384:512], ACT.Copy)
                    n.then_inc(s_PT, 1)
                attn_hi(act, hp, 11)
            for i in range(4):
                act.wait_ge(s_lnd, 2 * i + 2)
                if i >= 2:
                    act.wait_ge(s_lns, i)
                y = convy[:, i]
                nc.scalar.activation(lnt[:, i % 2, 0:LAT], y[:, 0:LAT], ACT.Square).then_inc(s_lnp, 1)
                nc.scalar.activation(lnt[:, i % 2, LAT:T], y[:, 542:798], ACT.Square).then_inc(s_lnp, 1)
            act.wait_ge(s_lns, 5)
            nc.scalar.activation(lnm[:, 0], SSB, ACT.Ln, scale=1.0 / 512, bias=eps[:]).then_inc(s_lna, 1)
            act.wait_ge(s_lna, 1)
            nc.scalar.activation(lnm[:, 0], lnm[:, 0], ACT.Exp, scale=-0.5).then_inc(s_lna, 1)
            for i in range(4):
                act.wait_ge(s_lnd, 8 + 2 * i + 2)
                if i:
                    act.wait_ge(s_cat, i)
                nc.scalar.activation(lnm[:, 1], lnt[:, i % 2], ACT.Silu, scale=sm("ln_g", i), bias=sm("ln_b", i)).then_inc(s_lna, 1)
                act.wait_ge(s_lna, 2 * i + 3)
                nc.scalar.activation(c_hi[:, 4 + i], lnm[:, 1], ACT.Copy).then_inc(s_lna, 1)
            act.wait_ge(s_cat, 4)
            act.dma_start(X[:], A["xT"]).then_inc(s_x, 16)
            out_proj(0)
            norm(1)
            ffn(0)
            for j in range(2):
                act.wait_ge(s_gf[j], XUP[2] // 2)
            act.dma_start(x_spill, X[:, :, 0:LAT]).then_inc(s_spill, 16)
            norm(2)
            act.wait_ge(s_h, 24)
            act.dma_start(wg_raw, A["gate_w"]).then_inc(s_gw, 16)
            act.dma_start(gb, A["gate_b"].partition_broadcast(128)).then_inc(s_gw, 16)
            act.wait_ge(s_gw, 32)
            nc.scalar.activation(wg_hi[:].rearrange("p k n -> p (k n)"), wg_raw, ACT.Copy).then_inc(s_wgh, 1)
            act.wait_ge(s_g2, 2)
            nc.scalar.activation(bb[:, 0], bb[:, 0], ACT.Exp).then_inc(s_g3, 1)
            act.wait_ge(s_g3, 1)
            nc.scalar.activation(bb[:, 0], bb[:, 0], ACT.Ln, bias=1.0).then_inc(s_g3, 1)
            act.wait_ge(s_g2, 58)
            nc.scalar.activation(ge[:].rearrange("p a n -> p (a n)"), ge[:].rearrange("p a n -> p (a n)"), ACT.Exp)\
                .then_inc(s_g3, 1)
            for hp in range(4):
                r = R_ML + 4 * hp
                half = r // 2
                split_hi(act, half, 1)
                act.wait_ge(s_gemm, r + 1)
                if hp == 0:
                    act.wait_ge(s_pad, 5)
                nc.scalar.activation(qpad[:, 2:2 + LAT], G[0][:, 0:LAT], ACT.Copy).then_inc(s_gf[0], 1)
                split_hi(act, half + 1, 0)
                act.wait_ge(s_gemm, r + 2)
                nc.scalar.activation(kpad[:, 2:2 + LAT], G[1][:, 0:LAT], ACT.Copy)
                nc.scalar.activation(kpad[:, LAT + 6:T + 6], G[1][:, LAT:T], ACT.Copy).then_inc(s_gf[1], 1)
                split_hi(act, half + 1, 1)
                act.wait_ge(s_mcv, 10 * hp + 5)
                nc.scalar.activation(qs[:], qs[:], ACT.Silu, bias=sm("mconv_b", hp)).then_inc(s_sil, 1)
                act.wait_ge(s_mcv, 10 * hp + 10)
                nc.scalar.activation(ks[:], ks[:], ACT.Silu, bias=sm("mconv_b", 4 + hp)).then_inc(s_sil, 1)
                for h in range(2):
                    act.wait_ge(s_gemm, r + 3 + h)
                    if 2 * hp + h:
                        act.wait_ge(s_vtp, 2 * hp + h)
                    nc.scalar.activation(vt1[:], G[h][:, 0:T], ACT.Copy).then_inc(s_gf[h], 1)
                    if h == 0:
                        split_hi(act, half + 2, 0)
                for u in range(4):
                    n, h, d, H = 4 * hp + u, u // 2, u % 2, 2 * hp + u // 2
                    act.wait_ge(s_R, n + 1)
                    if n:
                        act.wait_ge(s_Pm, n)
                        act.wait_ge(s_qi, n)
                    for c in range(CH):
                        col = 48 * d + 8 * c + H
                        nc.scalar.activation(Eb[:, 128 * c:128 * c + 128], PS[:, 5, 128 * c:128 * c + 128],
                                             ACT.Relu, bias=nga[:, col:col + 1]).then_inc(s_rel, 1)
                    act.wait_ge(s_rel, 4 * n + 4)
                    nc.scalar.activation(Eb[:], Eb[:], ACT.Exp, scale=-1.0).then_inc(s_E2, 1)
                    hr = slice(64 * h, 64 * h + 64)
                    for c in range(CH):
                        col = 48 * d + 8 * c + H
                        nc.scalar.activation(ib[hr, 128 * c:128 * c + 128], PS[hr, 5, 128 * c:128 * c + 128],
                                             ACT.Exp, scale=-1.0, bias=mB[hr, col:col + 1]).then_inc(s_ib, 1)
                act.wait_ge(s_rna, 4 * hp + 4)
                sq8 = ssq[:].rearrange("p h c -> p (h c)")
                nc.scalar.activation(sq8, sq8, ACT.Ln, scale=1.0 / 128, bias=eps[:]).then_inc(s_rn, 1)
                act.wait_ge(s_rn, 2 * hp + 1)
                nc.scalar.activation(sq8, sq8, ACT.Exp, scale=-0.5).then_inc(s_rn, 1)
            for o in range(8):
                r = R_GATE + o
                split_hi(act, (r + 1) // 2, (r + 1) % 2)
                act.wait_ge(s_gemm, r + 1)
                if o >= 2:
                    act.wait_ge(s_otmp, o - 1)
                nc.scalar.activation(Pm[:, o % 2], G[o % 2][:, 0:LAT], ACT.Sigmoid).then_inc(s_gf[o % 2], 1)
                act.wait_ge(s_otmp, o + 1)
                nc.scalar.activation(c_hi[:, o, 0:LAT], qi[:, o % 2], ACT.Copy).then_inc(s_ohi, 1)
            act.wait_ge(s_hT, 8)
            act.dma_start(X[:, :, 0:LAT], x_spill).then_inc(s_back, 16)
            out_proj(1)
            norm(3)
            ffn(1)
            for j in range(2):
                act.wait_ge(s_gf[j], NR // 2)
            act.dma_start(out, X[:, :, 0:LAT]).then_inc(s_out, 16)
            act.wait_ge(s_spill, 16)
            act.wait_ge(s_out, 16)

        @block.vector
        def _(dve):
            V = nc.vector

            def norm(w):
                cols = NORM_T[w]
                if w == 0:
                    dve.wait_ge(s_x, 16)
                dve.wait_ge(s_nrs, w + 1)

                def scaled(k):
                    V.tensor_tensor(nt[:, k % 2, 0:cols], X[:, k, 0:cols], nrs[:, 0:cols], ALU.mult).then_inc(s_nt, 1)
                scaled(0)
                for k in range(KT):
                    n = 8 * w + k
                    if k + 1 < KT:
                        if k >= 1:
                            dve.wait_ge(s_nhi, n)
                        scaled(k + 1)
                    dve.wait_ge(s_nhi, n + 1)
                    V.tensor_tensor(h_lo[:, k, 0:cols], nt2[:, k % 2, 0:cols], h_hi[:, k, 0:cols].bitcast(f32),
                                    ALU.subtract).then_inc(s_h, 1)

            def mod_add(a, n, src):
                b = small[:, SM["ada_b"][0]:SM["ada_b"][1]]
                V.tensor_tensor(mod[:, a:a + n], src, b[:, a:a + n, None].to_broadcast([128, n, 2]), ALU.add)\
                    .then_inc(s_mod, 1)

            def gain(w, g):
                V.scalar_tensor_tensor(out=amod[:, w], in0=mod[:, NORM_SC[w]:NORM_SC[w] + 8], scalar=1.0,
                                       in1=g[:, :, None].to_broadcast([128, 8, 2]), op0=ALU.add, op1=ALU.mult)\
                    .then_inc(s_amod, 1)

            def residual(half, j, o, gate, segs):
                dve.wait_ge(s_gemm, 2 * half + (j + 1))
                dve.wait_ge(s_gf[j], half)
                for s, a, b in segs:
                    xs = X[:, bass.ds(o, 1), a:b].rearrange("p a n -> p (a n)")
                    gv = mod[:, bass.ds(o + gate, 1), s:s + 1].rearrange("p a n -> p (a n)")
                    i = V.scalar_tensor_tensor(out=xs, in0=G[j][:, a:b], scalar=gv, in1=xs, op0=ALU.mult, op1=ALU.add)
                    i.then_inc(s_gf[j] if b == segs[-1][2] else s_xpart, 1)

            def ffn(layer):
                cols = T if layer == 0 else LAT
                segs = norm_cols(2 * layer + 1) if layer == 0 else ((0, 0, LAT),)
                R = R_F0 if layer == 0 else R_F1
                for g, (f0, nf) in enumerate(GROUPS):
                    with dve.Fori(0, nf) as i:
                        half = dve.snap(i + R // 2)
                        n = dve.snap(i + layer * FT + f0)
                        split_lo(dve, half, 1)
                        split_lo(dve, half + 1, 0)
                        dve.wait_ge(s_gf[0], half + 1)
                        dve.wait_ge(s_gemm, 2 * half + 2)
                        V.tensor_tensor(ftmp[:, 0:cols], G[1][:, 0:cols], sg[:, 0:cols], ALU.mult).then_inc(s_gf[1], 1)
                        dve.wait_ge(s_hhi, n + 1)
                        V.tensor_tensor(c_lo[:, bass.ds(i, 1), 0:cols].rearrange("p a n -> p (a n)"), ftmp[:, 0:cols],
                                        c_hi[:, bass.ds(i, 1), 0:cols].bitcast(f32).rearrange("p a n -> p (a n)"),
                                        ALU.subtract).then_inc(s_hid, 1)
                    R += 2 * nf
                    last = 1 if (layer == 1 and g == 2) else 0
                    with dve.Fori(0, 4 - last) as i:
                        half = dve.snap(i + R // 2)
                        o = dve.snap(2 * i)
                        split_lo(dve, half, 1)
                        residual(half, 0, o, 48 * layer + G2, segs)
                        split_lo(dve, half + 1, 0)
                        residual(half, 1, o + 1, 48 * layer + G2, segs)
                        if layer == 0:
                            a = dve.snap(4 * i + (48 + 16 * g))
                            dve.wait_ge(s_adm, a + 4)
                            b = small[:, SM["ada_b"][0]:SM["ada_b"][1]]
                            V.tensor_tensor(mod[:, bass.ds(a, 4)], ADQ.rearrange("p (a s) -> p a s", s=2),
                                            b[:, bass.ds(a, 4)][:, :, None].to_broadcast([128, 4, 2]), ALU.add)\
                                .then_inc(s_mod, 1)
                    if last:
                        half = (NR - 2) // 2
                        split_lo(dve, half, 1)
                        residual(half, 0, 6, 48 * layer + G2, segs)
                        residual(half, 1, 7, 48 * layer + G2, segs)
                    R += 8

            def out_proj(layer, segs):
                R = R_O0 if layer == 0 else R_O1
                with dve.Fori(0, 4) as i:
                    half = dve.snap(i + R // 2)
                    o = dve.snap(2 * i)
                    split_lo(dve, half, 1)
                    residual(half, 0, o, 48 * layer + G1, segs)
                    split_lo(dve, half + 1, 0)
                    residual(half, 1, o + 1, 48 * layer + G1, segs)

            V.memset(eps[:], EPS).then_inc(s_eps, 1)
            dve.wait_ge(s_small, 16)
            V.tensor_scalar(qg8[:], sm("q_g", 0), 0.125, None, ALU.mult).then_inc(s_q8, 1)
            dve.wait_ge(s_adm, 16)
            mod_add(0, 16, ADP[:, 0:32].rearrange("p (a s) -> p a s", s=2))
            dve.wait_ge(s_mod, 1)
            gain(0, sm("mix_g", 0, 8))
            norm(0)
            split_lo(dve, 0, 0)
            for i in range(4):
                split_lo(dve, (i + 1) // 2, (i + 1) % 2)
                dve.wait_ge(s_vX, i + 1)
                V.tensor_copy(Vt[:, 0:5, 128 * i:128 * i + 128],
                              PSf[:, 2048:2048 + 640].rearrange("p (b f) -> p b f", b=5)).then_inc(s_v, 1)
                V.tensor_copy(Vt[0:64, 5:7, 128 * i:128 * i + 128],
                              PSf[0:64, 2048 + 640:2048 + 896].rearrange("p (b f) -> p b f", b=2)).then_inc(s_v, 1)
            dve.wait_ge(s_q8, 1)
            dve.wait_ge(s_zero, 2)
            cs = [0]

            def conv_steps(hp, n):
                for _ in range(n):
                    j = cs[0] - TAPS * hp
                    if j >= TAPS:
                        return
                    y, src, w = convy[:, hp], glu[:, j:j + 798], sm("conv_w", TAPS * hp + j)
                    if j:
                        dve.wait_ge(s_conv, cs[0])
                        V.scalar_tensor_tensor(out=y, in0=src, scalar=w, in1=y, op0=ALU.mult, op1=ALU.add)\
                            .then_inc(s_conv, 1)
                    else:
                        dve.wait_ge(s_gf[0], R_AB // 2 + 2 * hp + 2)
                        V.tensor_scalar(y, src, w, sm("conv_b", hp), ALU.mult, ALU.add).then_inc(s_conv, 1)
                    cs[0] += 1

            def attn_lo(hp, u):
                h, t, U = u // 6, u % 6, 12 * hp + u
                dve.wait_ge(s_ahi, U + 1)
                dst, src = attn_views(c_lo, hp, h, t, U)
                hi, _ = attn_views(c_hi, hp, h, t, U)
                V.tensor_tensor(dst, src, hi.bitcast(f32), ALU.subtract).then_inc(s_alo, 1)

            for hp in range(4):
                r = R_AB + 4 * hp
                half = r // 2
                split_lo(dve, half, 1)
                split_lo(dve, half + 1, 0)
                for x in range(2):
                    dve.wait_ge(s_rs, 2 * hp + x + 1)
                    g, rs, gn = G[x], rsb[:, x], (qg8[:], sm("k_g", 0))[x]
                    gr = g[:, 0:LAT].rearrange("p (a c) -> p a c", a=ROWS)
                    rr = rs[:, 0:LAT].rearrange("p (a c) -> p a c", a=ROWS)

                    def scale(dst, a, b):
                        return V.scalar_tensor_tensor(out=dst, in0=a, scalar=gn, in1=b, op0=ALU.mult, op1=ALU.mult)
                    if x == 0:
                        scale(qB[:, 0:LAT].rearrange("p (c a) -> p a c", a=ROWS), gr, rr)
                        scale(qB[:, LAT:T], g[:, LAT:T], rs[:, LAT:T]).then_inc(s_gf[x], 1)
                    else:
                        for b, n in enumerate((8, 16, 16, 16, 8)):
                            c0 = (0, 8, 24, 40, 56)[b]
                            scale(kB[:, KB_OFF[b]:KB_OFF[b] + 8 * n].rearrange("p (a c) -> p a c", a=ROWS),
                                  gr[:, :, c0:c0 + n], rr[:, :, c0:c0 + n])
                        scale(kB[:, LAT:T], g[:, LAT:T], rs[:, LAT:T]).then_inc(s_gf[x], 1)
                split_lo(dve, half + 1, 1)
                dve.wait_ge(s_gf[1], half + 2)
                if hp:
                    dve.wait_ge(s_conv, TAPS * hp)
                V.tensor_tensor(glu[:, 15:15 + LAT], G[0][:, 0:LAT], sgm[:, 0:LAT], ALU.mult)
                V.tensor_tensor(glu[:, 557:557 + CTX], G[0][:, LAT:T], sgm[:, LAT:T], ALU.mult).then_inc(s_gf[0], 1)
                split_lo(dve, half + 2, 0)
                for u in range(12):
                    h, t, U = u // 6, u % 6, 12 * hp + u
                    H = 2 * hp + h
                    nk = 256 + sum(b[2] for b in key_blocks(t)[2:])
                    dve.wait_ge(s_S, U + 1)
                    m, ng, rsum = atmp[:, U % 2:U % 2 + 1], atmp[:, 2 + U % 2:3 + U % 2], atmp[:, 4 + U % 2:5 + U % 2]
                    if t < 4:
                        dve.wait_ge(s_bx, 8 * (H + 1))
                        if U >= 2:
                            dve.wait_ge(s_Tr, U - 1)
                        kind = (0, 1, 1, 2)[t]
                        V.tensor_tensor_reduce(out=Pb[:, U % 2, 0:nk], in0=PS[:, 4 + U % 2, 0:nk],
                                               in1=bx[:, BX[kind]:BX[kind] + nk], scale=1.0, scalar=-3e38,
                                               op0=ALU.add, op1=ALU.max, accum_out=m).then_inc(s_mx, 1)
                        dve.wait_ge(s_mx, 4 * H + t + 1)
                        V.tensor_scalar(ng, m, -1.0, None, ALU.mult).then_inc(s_neg, 1)
                    else:
                        V.tensor_reduce(out=ng, in_=PS[:, 4 + U % 2, 0:nk], axis=AX.X, op=ALU.max, negate=True)\
                            .then_inc(s_neg, 1)
                    conv_steps(hp, 3 if u < 7 else 2)
                    dve.wait_ge(s_E, U + 1)
                    V.reciprocal(atmp[:, 6 + U % 2:7 + U % 2], rsum).then_inc(s_rr, 1)
                    dve.wait_ge(s_rr, U + 1)
                    V.tensor_scalar(Pb[:, U % 2, 0:nk], Pb[:, U % 2, 0:nk], atmp[:, 6 + U % 2:7 + U % 2], None, ALU.mult)\
                        .then_inc(s_Pn, 1)
                    if u:
                        attn_lo(hp, u - 1)
                attn_lo(hp, 11)
                mod_add(16 + 8 * hp, 8, ADM.rearrange("p (a s) -> p a s", s=2))
            assert cs[0] == 4 * TAPS
            dve.wait_ge(s_mod, 5)
            gain(1, sm("ffn_g", 0, 8))
            dve.wait_ge(s_lns, 1)
            for i in range(4):
                for y, m in ((convy[:, i, 0:LAT], SSA[:, 0:LAT]), (convy[:, i, 542:798], SSA[:, LAT:T])):
                    V.scalar_tensor_tensor(out=y, in0=m, scalar=-1.0 / 512, in1=y, op0=ALU.mult, op1=ALU.add)\
                        .then_inc(s_lnd, 1)
            dve.wait_ge(s_lnd, 8)
            dve.wait_ge(s_lna, 2)
            for i in range(4):
                if i >= 2:
                    dve.wait_ge(s_lna, 2 * i)
                for (a, b), y in (((0, LAT), convy[:, i, 0:LAT]), ((LAT, T), convy[:, i, 542:798])):
                    V.tensor_tensor(lnt[:, i % 2, a:b], y, lnm[:, 0, a:b], ALU.mult).then_inc(s_lnd, 1)
                dve.wait_ge(s_lna, 2 * i + 4)
                V.tensor_tensor(c_lo[:, 4 + i], lnm[:, 1], c_hi[:, 4 + i].bitcast(f32), ALU.subtract).then_inc(s_cat, 1)
            dve.wait_ge(s_x, 32)
            out_proj(0, norm_cols(0))
            norm(1)
            ffn(0)
            dve.wait_ge(s_mod, 17)
            gain(2, sm("mix_g", 8, 8))
            gain(3, sm("ffn_g", 8, 8))
            norm(2)
            dve.wait_ge(s_wgh, 1)
            V.tensor_tensor(wg_lo[:].rearrange("p k n -> p (k n)"), wg_raw,
                            wg_hi[:].rearrange("p k n -> p (k n)").bitcast(f32), ALU.subtract).then_inc(s_wgl, 1)
            g2 = [0]

            def step(i):
                g2[0] += 1
                i.then_inc(s_g2, 1)
                dve.wait_ge(s_g2, g2[0])

            def dch(v):
                return v.rearrange("p (d c h) -> p d c h", d=2, c=NC)

            dve.wait_ge(s_g1, 1)
            step(V.tensor_tensor(gall[:], PS[:, 4, 0:192].rearrange("p (c n) -> p c n", c=NC),
                                 gb[:, None, :].to_broadcast([128, NC, 32]), ALU.add))
            fg = gall[:, :, 16:32]
            b0 = bb[:, 0].rearrange("p (c n) -> p c n", c=NC)
            step(V.scalar_tensor_tensor(out=b0, in0=fg, scalar=-1.0, in1=fg, op0=ALU.mult, op1=ALU.min))
            dve.wait_ge(s_g3, 2)
            for d in range(2):
                i = V.scalar_tensor_tensor(out=lf[:, d], in0=fg[:, :, 8 * d:8 * d + 8], scalar=0.0,
                                           in1=b0[:, :, 8 * d:8 * d + 8], op0=ALU.min, op1=ALU.subtract)
            step(i)
            dve.wait_ge(s_g1, 2)
            step(V.tensor_copy(bb[:].rearrange("p a n -> p (a n)"), PS[:, 5, 0:192]))
            step(V.tensor_tensor(dch(ga[:]), gall[:, :, 0:16].rearrange("p c (d h) -> p d c h", d=2), dch(bb[:, 0]),
                                 ALU.subtract))
            dve.wait_ge(s_g1, 3)
            step(V.tensor_copy(arow[0:48].rearrange("p a n -> p (a n)"), PS[0:48, 6, 0:256]))
            step(V.tensor_reduce(out=mx48[0:48], in_=arow[0:48], axis=AX.X, op=ALU.max))
            for d in range(2):
                step(V.tensor_tensor_scan(cmrow[0:48, d], arow[0:48, d], arow[0:48, d], -3e38, ALU.max, ALU.max))
            for d in range(2):
                step(V.tensor_scalar(dM[0:48, d], ident[0:48, 0:48], mx48[0:48, d:d + 1], None, ALU.mult))
            dve.wait_ge(s_g1, 4)
            step(V.tensor_copy(gM, PS[:, 7, 0:96]))
            step(V.tensor_copy(gcm[:].rearrange("p a n -> p (a n)"), PS[:, 7, 96:192]))
            ORDER = ((4, 5, 0, 1, 2, 3), (5, 4, 3, 2, 1, 0))

            def at8(v, d, c):
                return v[:, 48 * d + 8 * c:48 * d + 8 * c + 8]
            for d in range(2):
                step(V.memset(at8(mB, d, ORDER[d][0]), 0.0))
            for s in range(NC):
                for d in range(2):
                    c = ORDER[d][s]
                    step(V.tensor_tensor(at8(mA, d, c), at8(mB, d, c), at8(gM, d, c), ALU.max))
                    step(V.tensor_tensor(at8(mA, d, c), at8(mA, d, c), at8(bb[:, 1], d, c), ALU.add))
                    if s + 1 < NC:
                        step(V.tensor_copy(at8(mB, d, ORDER[d][s + 1]), at8(mA, d, c)))
            dve.wait_ge(s_g1, 5)
            step(V.tensor_copy(gcm[:, 1], PS[:, 4, 0:48]))
            step(V.tensor_tensor(rcol, mB, gcm[:].rearrange("p a n -> p (a n)"), ALU.max))
            step(V.tensor_tensor(ge[:, 0], bb[:, 1], mB, ALU.add))
            step(V.tensor_tensor(ge[:, 0], ge[:, 0], mA, ALU.subtract))
            step(V.tensor_tensor(ge[:, 1], bb[:, 1], ga, ALU.add))
            step(V.tensor_tensor(ge[:, 1], ge[:, 1], mA, ALU.subtract))
            step(V.tensor_tensor(ge[:, 2], bb[:, 0], rcol, ALU.add))
            step(V.tensor_scalar(nga, ga, -1.0, None, ALU.mult))
            step(V.tensor_scalar(ge[:, 2], ge[:, 2], -1.0, None, ALU.mult))
            assert g2[0] == 58, g2[0]
            dve.wait_ge(s_g1, 6)
            step(V.tensor_copy(nrow[0:48].rearrange("p a n -> p (a n)"), PS[0:48, 5, 192:448]))
            assert g2[0] == GD_END
            for v in (qpad[:, 0:2], qpad[:, LAT + 2:LAT + 4], kpad[:, 0:2], kpad[:, LAT + 2:LAT + 6],
                      kpad[:, T + 6:T + 8]):
                V.memset(v, 0.0).then_inc(s_pad, 1)
            V.memset(vaug[:, :, :, 128:129], 1.0).then_inc(s_pad, 1)
            dve.wait_ge(s_pad, 6)
            dve.wait_ge(s_spill, 16)
            dve.wait_ge(s_g3, 3)
            cos, sin = cn("cos"), cn("sin")
            mc, st, rna, dn = [0], [0], [0], [0]

            def chain(i, sm_, n):
                n[0] += 1
                i.then_inc(sm_, 1)
                dve.wait_ge(sm_, n[0])

            def finish(n):
                hp, h, d = n // 4, n % 4 // 2, n % 2
                H = 2 * hp + h
                dve.wait_ge(s_num, n + 1)
                num = PS[:, 6:8, 0:258].rearrange("p b (x v) -> p b x v", v=129)
                dd = den[:, 0].rearrange("p (b x) -> p b x", b=2)
                enm = ge[:, 2].rearrange("p (d c h) -> p d c h", d=2, c=NC)[:, d, 0:CH, H]
                nd = num[:, :, :, 128]
                chain(V.scalar_tensor_tensor(out=dd, in0=nd, scalar=-1.0, in1=enm.rearrange("p (b x) -> p b x", b=2),
                                             op0=ALU.mult, op1=ALU.max), s_den, dn)
                chain(V.tensor_tensor(dd, nd, dd, ALU.max), s_den, dn)
                chain(V.reciprocal(den[:, 1], den[:, 0]), s_den, dn)
                rb = den[:, 1].rearrange("p (b x) -> p b x", b=2)[:, :, :, None].to_broadcast([128, 2, 2, 128])
                if d == 0:
                    V.tensor_tensor(hsum[:, :, H].rearrange("p (b x) v -> p b x v", b=2), num[:, :, :, 0:128], rb, ALU.mult)\
                        .then_inc(s_hs, 1)
                else:
                    V.tensor_tensor(mt[:].rearrange("p (b x v) -> p b x v", b=2, x=2), num[:, :, :, 0:128], rb, ALU.mult)\
                        .then_inc(s_hs, 1)
                    dve.wait_ge(s_hs, n + 1)
                    V.tensor_tensor(hsum[:, :, H], hsum[:, :, H], mt[:].rearrange("p (c v) -> p c v", c=CH), ALU.add)\
                        .then_inc(s_ha, 1)

            for hp in range(4):
                r = R_ML + 4 * hp
                half = r // 2
                split_lo(dve, half, 1)
                for x, (pad, y, n) in enumerate(((qpad, qs, LAT), (kpad, ks, LAT + 4 + CTX))):
                    dve.wait_ge(s_gf[x], half + 1)
                    for j in range(MTAPS):
                        w = sm("mconv_w", MTAPS * (4 * x + hp) + j)
                        if j == 0:
                            i = V.tensor_scalar(y[:], pad[:, 0:n], w, None, ALU.mult)
                        else:
                            i = V.scalar_tensor_tensor(out=y[:], in0=pad[:, j:j + n], scalar=w, in1=y[:],
                                                       op0=ALU.mult, op1=ALU.add)
                        chain(i, s_mcv, mc)
                    split_lo(dve, half + 1, x)
                for x, (y, z, bank, sc) in enumerate(((qs, qr, 4, 0.125), (ks, kr, 5, 1.0))):
                    dve.wait_ge(s_rot, 2 * hp + x + 1)
                    V.scalar_tensor_tensor(out=mt[:], in0=PS[:, bank, :], scalar=sc, in1=sin, op0=ALU.mult, op1=ALU.mult)\
                        .then_inc(s_rope, 1)
                    V.scalar_tensor_tensor(out=z[:], in0=y[:, 0:LAT], scalar=sc, in1=cos, op0=ALU.mult, op1=ALU.mult)\
                        .then_inc(s_rope, 1)
                    dve.wait_ge(s_rope, 6 * hp + 3 * x + 2)
                    V.tensor_tensor(z[:], z[:], mt[:], ALU.add).then_inc(s_rope, 1)
                    dve.wait_ge(s_rope, 6 * hp + 3 * x + 3)
                dve.wait_ge(s_kT, hp + 1)
                for d in range(2):
                    wk = ge[:, 1].rearrange("p (d c h) -> p d c h", d=2, c=NC)[:, d, :, 2 * hp:2 * hp + 2]
                    V.tensor_tensor(kw[:, d].rearrange("p c (h k) -> p c h k", h=2),
                                    PSf[:, 3072:3072 + T].rearrange("p (c h k) -> p c h k", c=NC, h=2),
                                    wk[:, :, :, None].to_broadcast([128, NC, 2, 64]), ALU.mult).then_inc(s_kw, 1)
                for h in range(2):
                    dve.wait_ge(s_vtp, 2 * hp + h + 1)
                    V.tensor_copy(vaug[:, h, :, 0:128], (SSA, SSB)[h].rearrange("p (c v) -> p c v", c=NC)).then_inc(s_va, 1)
                for h in range(2):
                    hr = slice(64 * h, 64 * h + 64)
                    dec = ge[hr, 0].rearrange("p (d c h) -> p d c h", d=2, c=NC)[:, :, :, 2 * hp + h]
                    chain(V.tensor_copy(dcomb[hr], dec), s_st, st)
                dve.wait_ge(s_su, 2 * hp + 1)
                for d in range(2):
                    if d:
                        dve.wait_ge(s_su, 2 * hp + 2)
                    for s in range(NC - 1):
                        su = PS[:, 4 + 2 * d + s // 3, 129 * (s % 3):129 * (s % 3) + 129]
                        if s == 0:
                            i = V.tensor_copy(Sst[:, d, 1], su)
                        else:
                            c = ORDER[d][s]
                            i = V.scalar_tensor_tensor(out=Sst[:, d, s + 1], in0=Sst[:, d, s], scalar=dcomb[:, d, c:c + 1],
                                                       in1=su, op0=ALU.mult, op1=ALU.add)
                        chain(i, s_st, st)
                split_lo(dve, half + 2, 0)
                for u in range(4):
                    n, h, d = 4 * hp + u, u // 2, u % 2
                    hr = slice(64 * h, 64 * h + 64)
                    dve.wait_ge(s_kq, 2 * hp + h + 1)
                    if n:
                        dve.wait_ge(s_Pm, n)
                    mask = cn(("upto", "from")[d])[:, None, :].to_broadcast([128, CH, 128])
                    V.tensor_tensor(kqm[:].rearrange("p (c i) -> p c i", c=CH),
                                    PS[:, 4].rearrange("p (c i) -> p c i", c=CH), mask, ALU.mult).then_inc(s_km, 1)
                    dve.wait_ge(s_km, n + 1)
                    dve.wait_ge(s_E2, n + 1)
                    if n >= 2:
                        dve.wait_ge(s_num, n - 1)
                    V.tensor_tensor(Pm[:, n % 2], Eb[:], kqm[:], ALU.mult).then_inc(s_Pm, 1)
                    dve.wait_ge(s_ib, 4 * n + 4)
                    V.tensor_tensor(qi[hr, n % 2], qr[hr], ib[hr], ALU.mult).then_inc(s_qi, 1)
                    if u:
                        finish(n - 1)
                finish(4 * hp + 3)
                dve.wait_ge(s_ha, 2 * hp + 2)
                for h in range(2):
                    hv = hsum[:, :, 2 * hp + h]
                    chain(V.tensor_tensor(mt[:].rearrange("p (c v) -> p c v", c=CH), hv, hv, ALU.mult), s_rna, rna)
                    chain(V.tensor_reduce(out=ssq[:, h], in_=mt[:].rearrange("p (c v) -> p c v", c=CH), axis=AX.X,
                                          op=ALU.add), s_rna, rna)
                dve.wait_ge(s_rn, 2 * hp + 2)
                for h in range(2):
                    hv = hsum[:, :, 2 * hp + h]
                    V.tensor_tensor(hv, hv, ssq[:, h, :, None].to_broadcast([128, CH, 128]), ALU.mult).then_inc(s_hn, 1)
                dve.wait_ge(s_hn, 2 * hp + 2)
            for o in range(8):
                r = R_GATE + o
                split_lo(dve, (r + 1) // 2, (r + 1) % 2)
                dve.wait_ge(s_hT, o + 1)
                dve.wait_ge(s_gf[o % 2], r // 2 + 1)
                if o >= 2:
                    dve.wait_ge(s_ohi, o - 1)
                    dve.wait_ge(s_ocat, o - 1)
                V.scalar_tensor_tensor(out=qi[:, o % 2], in0=PS[:, 4 + o % 2], scalar=sm("mnorm_g", o), in1=Pm[:, o % 2],
                                       op0=ALU.mult, op1=ALU.mult).then_inc(s_otmp, 1)
                dve.wait_ge(s_ohi, o + 1)
                V.tensor_tensor(c_lo[:, o, 0:LAT], qi[:, o % 2], c_hi[:, o, 0:LAT].bitcast(f32), ALU.subtract)\
                    .then_inc(s_ocat, 1)
            dve.wait_ge(s_back, 16)
            out_proj(1, ((0, 0, LAT),))
            norm(3)
            ffn(1)

        @block.tensor
        def _(pe):
            MM = nc.tensor.matmul

            def norm(w):
                for k in range(KT):
                    n = 8 * w + k
                    pe.wait_ge(s_nsq, n + 1)
                    for _, a, b in norm_cols(w):
                        last = MM(SSA[:, a:b], ones, nt[:, k % 2, a:b], start=(k == 0), stop=(k == KT - 1))
                    last.then_inc(s_nss, 1)

            def ada(a, w, dst):
                for k in range(KT):
                    last = MM(dst, w[:, 128 * k:128 * k + 128], sT[:, k], start=(k == 0), stop=(k == KT - 1))
                last.then_inc(s_adm, 1)

            def ffn(layer):
                cols = LAY_COLS[layer]
                R = R_F0 if layer == 0 else R_F1
                for g, (f0, nf) in enumerate(GROUPS):
                    with pe.Fori(0, nf) as i:
                        half = pe.snap(i + R // 2)
                        product(pe, half, 0, h_hi, h_lo, cols)
                        product(pe, half, 1, h_hi, h_lo, cols)
                    R += 2 * nf
                    pe.wait_ge(s_hid, layer * FT + f0 + nf)
                    with pe.Fori(0, 4) as i:
                        half = pe.snap(i + R // 2)
                        na = pe.snap(i + 4 * g)
                        for j in range(2):
                            product(pe, half, j, c_hi, c_lo, cols, nf)
                            if layer == 0:
                                for q in range(2):
                                    if j == 0 and q == 0:
                                        pe.wait_ge(s_mod, na + 5)
                                    pe.wait_ge(s_adl[q], 16 * (2 * na + 16 + j) + 16)
                                    ada(0, adaw[:, q], ADQ[:, 4 * j + 2 * q:4 * j + 2 * q + 2])
                    R += 8

            def out_proj(layer):
                R = R_O0 if layer == 0 else R_O1
                with pe.Fori(0, 4) as i:
                    half = pe.snap(i + R // 2)
                    for j in range(2):
                        product(pe, half, j, c_hi, c_lo, LAY_COLS[layer])

            pe.wait_ge(s_sT, 1)
            for a in range(16):
                if a % 4 == 0:
                    pe.wait_ge(s_ada0[a // 4], 16)
                ada(a, scr[:, 1024 * (a % 8):1024 * (a % 8) + 1024], ADP[:, 2 * a:2 * a + 2])
            pe.wait_ge(s_const, 16)
            norm(0)
            pe.wait_ge(s_h, 8)
            for i in range(4):
                product(pe, i // 2, i % 2, h_hi, h_lo, BOTH, first=(i < 2))
                if i:
                    transpose_v(pe, i - 1)
            transpose_v(pe, 3)
            for hp in range(4):
                r = R_AB + 4 * hp
                half = r // 2
                if hp:
                    pe.wait_ge(s_mod, hp + 1)
                product(pe, half, 0, h_hi, h_lo, BOTH)
                if hp:
                    pe.wait_ge(s_PT, 12 * hp)
                    pe.wait_ge(s_alo, 12 * hp)
                product(pe, half, 1, h_hi, h_lo, BOTH)
                for x in range(2):
                    pe.wait_ge(s_sq, 2 * hp + x + 1)
                    if x == 0:
                        if hp:
                            pe.wait_ge(s_E, 12 * hp)
                        else:
                            pe.wait_ge(s_v, 8)
                    if x == 1 and hp:
                        pe.wait_ge(s_PT, 12 * hp)
                        pe.wait_ge(s_alo, 12 * hp)
                    for a, b in BOTH:
                        last = MM((SSA, SSB)[x][:, a:b], cn("pair"), sqb[:, x, a:b], start=True, stop=True)
                    last.then_inc(s_ss, 1)
                product(pe, half + 1, 0, h_hi, h_lo, BOTH)
                product(pe, half + 1, 1, h_hi, h_lo, BOTH)

                def scores(u):
                    h, t, U = u // 6, u % 6, 12 * hp + u
                    hr = slice(64 * h, 64 * h + 64)
                    if u >= 2:
                        pe.wait_ge(s_E, U - 1)
                    q = qB[hr, 128 * t:128 * t + 128]
                    last = MM(PS[:, 4 + U % 2, 0:CTX], q, kB[hr, LAT:T], start=True, stop=True)
                    if t < 4:
                        k0, k1 = KB_OFF[t], (KB_OFF + (LAT,))[t + 2]
                        last = MM(PS[:, 4 + U % 2, 256:256 + k1 - k0], q, kB[hr, k0:k1], start=True, stop=True)
                    last.then_inc(s_S, 1)

                def attend(u):
                    h, t, U = u // 6, u % 6, 12 * hp + u
                    pe.wait_ge(s_PT, U + 1)
                    if u >= 2:
                        pe.wait_ge(s_alo, U - 1)
                    blocks = key_blocks(t)
                    for n, (b, _, size) in enumerate(blocks):
                        f = 128 * hp + 64 * h
                        last = MM(PS[64 * h:64 * h + 64, OB[U % 2], 0:128],
                                  Vt[0:size, VSLOT[b], f:f + 64], PTs[0:size, U % 2, 128 * n:128 * n + 128],
                                  start=(n == 0), stop=(n == len(blocks) - 1))
                    last.then_inc(s_O, 1)

                pe.wait_ge(s_rs, 2 * hp + 2)
                pe.wait_ge(s_gf[0], half + 1)
                pe.wait_ge(s_gf[1], half + 1)
                scores(0)
                for u in range(12):
                    h, t, U = u // 6, u % 6, 12 * hp + u
                    if u < 11:
                        scores(u + 1)
                    if u < 8:
                        a = 16 + 8 * hp + u
                        if u == 0:
                            pe.wait_ge(s_gf[0], half + 2)
                        pe.wait_ge(s_adl[a % 2], 16 * ((a - 16) // 2) + 16)
                        ada(a, adaw[:, a % 2], ADM[:, 2 * u:2 * u + 2])
                    pe.wait_ge(s_Pn, U + 1)
                    if u >= 2:
                        pe.wait_ge(s_PT, U - 1)
                    if u == 1:
                        pe.wait_ge(s_gf[1], half + 2)
                    blocks = key_blocks(t)
                    for n, (b, c, size) in enumerate(blocks):
                        last = nc.tensor.transpose(PS[0:size, PB[U % 2], 128 * n:128 * n + 128], Pb[:, U % 2, c:c + size], ident)
                    last.then_inc(s_Tr, 1)
                    if u:
                        attend(u - 1)
                attend(11)
            pe.wait_ge(s_conv, 4 * TAPS)
            pe.wait_ge(s_alo, 48)
            for i in range(4):
                y = convy[:, i]
                MM(SSA[:, 0:LAT], ones, y[:, 0:LAT], start=(i == 0), stop=(i == 3))
                last = MM(SSA[:, LAT:T], ones, y[:, 542:798], start=(i == 0), stop=(i == 3))
            last.then_inc(s_lns, 1)
            for i in range(4):
                pe.wait_ge(s_lnp, 2 * i + 2)
                for a, b in BOTH:
                    last = MM(SSB[:, a:b], ones, lnt[:, i % 2, a:b], start=(i == 0), stop=(i == 3))
                last.then_inc(s_lns, 1)
            pe.wait_ge(s_cat, 4)
            out_proj(0)
            norm(1)
            pe.wait_ge(s_h, 16)
            ffn(0)
            pe.wait_ge(s_mod, 17)
            norm(2)
            pe.wait_ge(s_h, 24)
            pe.wait_ge(s_wgl, 1)
            for c in range(NC):
                for k in range(KT):
                    for n, (x, w) in enumerate(((h_hi, wg_hi), (h_lo, wg_hi), (h_hi, wg_lo))):
                        last = MM(PS[:, 4, 32 * c:32 * c + 32], x[:, k, 128 * c:128 * c + 128], w[:, k],
                                  start=(k == 0 and n == 0), stop=(k == KT - 1 and n == 2))
            last.then_inc(s_g1, 1)
            pe.wait_ge(s_g2, 3)
            lff = lf[:].rearrange("p d c h -> p (d c h)")
            MM(PS[:, 5, 0:48], cn("upto"), lff[:, 0:48], start=True, stop=True)
            MM(PS[:, 5, 48:96], cn("from"), lff[:, 48:96], start=True, stop=True)
            MM(PS[:, 5, 96:192], ones, lff, start=True, stop=True).then_inc(s_g1, 1)
            pe.wait_ge(s_g2, 5)
            MM(PS[0:48, 6, 0:128], ga[:, 0:48], ident, start=True, stop=True)
            MM(PS[0:48, 6, 128:256], ga[:, 48:96], flip, start=True, stop=True).then_inc(s_g1, 1)
            pe.wait_ge(s_g2, 11)
            for d in range(2):
                MM(PS[:, 7, 48 * d:48 * d + 48], ones[0:48, :], dM[0:48, d], start=True, stop=True)
                last = MM(PS[:, 7, 96 + 48 * d:144 + 48 * d], cmrow[0:48, d], ident[0:48, 0:48], start=True, stop=True)
            last.then_inc(s_g1, 1)
            pe.wait_ge(s_g2, 13)
            MM(PS[:, 4, 0:48], flip, gcm[:, 1], start=True, stop=True).then_inc(s_g1, 1)
            pe.wait_ge(s_g2, 58)
            for d in range(2):
                last = MM(PS[0:48, 5, 192 + 128 * d:320 + 128 * d], rcol[:, 48 * d:48 * d + 48], ident, start=True, stop=True)
            last.then_inc(s_g1, 1)
            pe.wait_ge(s_g2, GD_END)
            ORDER = ((4, 5, 0, 1, 2, 3), (5, 4, 3, 2, 1, 0))
            STEP = ((2, 3, 4, 5), (5, 4, 3, 2))
            for hp in range(4):
                r = R_ML + 4 * hp
                half = r // 2
                product(pe, half, 0, h_hi, h_lo, ONLY)
                product(pe, half, 1, h_hi, h_lo, BOTH)
                product(pe, half + 1, 0, h_hi, h_lo, BOTH)
                for x, (y, bank) in enumerate(((qs, 4), (ks, 5))):
                    pe.wait_ge(s_sil, 2 * hp + x + 1)
                    if hp:
                        if x == 0:
                            pe.wait_ge(s_km, 4 * hp)
                        else:
                            pe.wait_ge(s_ib, 16 * hp)
                    MM(PS[:, bank], cn("rot"), y[:, 0:LAT], start=True, stop=True).then_inc(s_rot, 1)
                product(pe, half + 1, 1, h_hi, h_lo, BOTH)
                pe.wait_ge(s_rope, 6 * hp + 6)
                if hp:
                    pe.wait_ge(s_hs, 4 * hp)
                for c in range(NC):
                    src = kr[:, 128 * c:128 * c + 128] if c < CH else ks[:, 516 + 128 * (c - CH):644 + 128 * (c - CH)]
                    last = nc.tensor.transpose(PSf[:, 3072 + 128 * c:3200 + 128 * c], src, ident)
                last.then_inc(s_kT, 1)
                for h in range(2):
                    pe.wait_ge(s_gf[h], half + 2)
                    if h:
                        pe.wait_ge(s_kw, 2 * hp + 2)
                    for c in range(NC):
                        last = nc.tensor.transpose((SSA, SSB)[h][:, 128 * c:128 * c + 128], vt1[:, 128 * c:128 * c + 128], ident)
                    last.then_inc(s_vtp, 1)
                pe.wait_ge(s_va, 2 * hp + 2)
                pe.wait_ge(s_kw, 2 * hp + 2)
                for d in range(2):
                    for s in range(NC - 1):
                        c = ORDER[d][s]
                        for h in range(2):
                            last = MM(PS[64 * h:64 * h + 64, 4 + 2 * d + s // 3, 129 * (s % 3):129 * (s % 3) + 129],
                                      kw[:, d, c, 64 * h:64 * h + 64], vaug[:, h, c], start=True, stop=True)
                    last.then_inc(s_su, 1)
                pe.wait_ge(s_st, 12 * hp + 12)
                for u in range(4):
                    n, h, d = 4 * hp + u, u // 2, u % 2
                    hr = slice(64 * h, 64 * h + 64)
                    if d == 0:
                        if h:
                            pe.wait_ge(s_km, n)
                        for c in range(CH):
                            cc = slice(128 * c, 128 * c + 128)
                            last = MM(PS[:, 4, cc], kr[hr, cc], qr[hr, cc], start=True, stop=True)
                        last.then_inc(s_kq, 1)
                    pe.wait_ge(s_rs2, n + 1)
                    if u:
                        pe.wait_ge(s_ib, 4 * n)
                    MM(PS[:, 5], ones[0:48, :], rsel[0:48], start=True, stop=True).then_inc(s_R, 1)
                    pe.wait_ge(s_qi, n + 1)
                    pe.wait_ge(s_Pm, n + 1)
                    if u:
                        pe.wait_ge(s_hs, n)
                    for c in range(CH):
                        cc = slice(128 * c, 128 * c + 128)
                        dst = PS[:, 6 + c // 2, 129 * (c % 2):129 * (c % 2) + 129]
                        MM(dst, qi[hr, n % 2, cc], Sst[hr, d, STEP[d][c]], start=True, stop=False)
                        last = MM(dst, Pm[:, n % 2, cc], vaug[:, h, c], start=False, stop=True)
                    last.then_inc(s_num, 1)
            for o in range(8):
                r = R_GATE + o
                product(pe, r // 2, r % 2, h_hi, h_lo, ONLY)
                pe.wait_ge(s_hn, 8)
                if o < 2:
                    pe.wait_ge(s_km, 16)
                    pe.wait_ge(s_ib, 64)
                if o >= 2:
                    pe.wait_ge(s_otmp, o - 1)
                for c in range(CH):
                    last = nc.tensor.transpose(PS[:, 4 + o % 2, 128 * c:128 * c + 128], hsum[:, c, o], ident)
                last.then_inc(s_hT, 1)
            pe.wait_ge(s_ocat, 8)
            out_proj(1)
            norm(3)
            pe.wait_ge(s_h, 32)
            ffn(1)



def _chunks(w, tiles):
    K, N = w.shape
    v = w.reshape(K // 128, 128, N // 128, 128).transpose(2, 1, 0, 3).reshape(N // 128, 128, K)
    return v[np.asarray(tiles)]


def _ffn_chunks(wg, wu, wd):
    out = []
    g, u = _chunks(wg, range(FT)), _chunks(wu, range(FT))
    for f0, nf in GROUPS:
        out.append(np.stack([g[f0:f0 + nf], u[f0:f0 + nf]], 1).reshape(2 * nf, 128, 1024))
        d = _chunks(wd[128 * f0:128 * (f0 + nf)], range(KT))
        out.append(np.pad(d, ((0, 0), (0, 0), (0, 1024 - 128 * nf))))
    return out


def _columns(v):
    return np.ascontiguousarray(v.reshape(-1, 128).T)


def _layout(i):
    f = {k: np.asarray(v) for k, v in i.items()}
    ab, ml = f["ab_w_in"][0], f["ml_w_in"][0]
    w = [_chunks(ab, range(8, 12))]
    w += [_chunks(ab, (hp, 4 + hp, 12 + hp, 16 + hp)) for hp in range(4)]
    w += [_chunks(f["ab_w_out"][0], range(8))]
    w += _ffn_chunks(f["ffn_w_gate"][0], f["ffn_w_up"][0], f["ffn_w_down"][0])
    mlc = _chunks(ml[:, :3072], range(24))
    w += [mlc[[hp, 4 + hp, 8 + 2 * hp, 9 + 2 * hp]] for hp in range(4)]
    w += [mlc[16:24], _chunks(f["ml_w_out"][0], range(8))]
    w += _ffn_chunks(f["ffn_w_gate"][1], f["ffn_w_up"][1], f["ffn_w_down"][1])
    w = np.concatenate(w)
    assert w.shape == (NR, 128, 1024)
    tile2 = lambda v: np.concatenate([v, v])[:, None]
    small = np.concatenate([
        _columns(f["ada_b"]), _columns(f["norm_mix_g"]), _columns(f["norm_ffn_g"]),
        tile2(f["na_q_norm_g"][0]), tile2(f["na_k_norm_g"][0]),
        f["conv_w"][0].reshape(TAPS, 4, 128).transpose(2, 1, 0).reshape(128, 4 * TAPS),
        _columns(f["conv_b"]), _columns(f["conv_ln_g"]), _columns(f["conv_ln_b"]),
        f["ml_conv_w"][0].reshape(MTAPS, 8, 128).transpose(2, 1, 0).reshape(128, 8 * MTAPS),
        _columns(f["ml_conv_b"]), _columns(f["ml_norm_g"]),
        np.stack([f["c"][0].reshape(KT, 128), f["c_ctx"].reshape(KT, 128)], 2).transpose(1, 0, 2).reshape(128, 16),
    ], 1)
    assert small.shape == (128, NSM)
    rpb = np.pad(f["na_rpb"][0][::-1, ::-1].transpose(1, 0, 2), ((0, 0), (0, 0), (8, 9)))
    xT = np.concatenate([f["x"][0], f["ctx"][0]]).T.reshape(KT, 128, T).transpose(1, 0, 2)
    return {
        "w": w, "small": small, "rpb": rpb, "xT": xT, "const": _constants(),
        "ada": np.concatenate([_chunks(f["ada_w"][l], range(48)) for l in range(2)]),
        "gate_w": ml[:, 3072:].reshape(KT, 128, 32).transpose(1, 0, 2).reshape(128, 256),
        "gate_b": f["ml_gate_b"][0],
    }


def _constants():
    p = np.arange(128)
    eye = np.eye(128)
    rot = np.zeros((128, 128))
    for m in range(128):
        if m % 32 < 16:
            rot[m + 16, m] = -1.0
        else:
            rot[m - 16, m] = 1.0
    inv = np.float32(10000.0) ** (-(p % 16).astype(np.float32) / np.float32(16))
    t = np.arange(LAT)
    pos = np.where((p % 64 < 32)[:, None], (t // GRID)[None], (t % GRID)[None]).astype(np.float32)
    ang = pos * inv[:, None].astype(np.float32)
    c = np.concatenate([eye, eye[::-1], p[:, None] <= p[None], p[:, None] >= p[None],
                        (p[:, None] // 64) == (p[None] // 64), np.ones((128, 128)), rot, np.cos(ang), np.sin(ang)], 1)
    return c.astype(np.float32)


def kernel(**inputs):
    import concourse.bacc as bacc
    from concourse.bass_utils import run_bass_kernel_spmd

    nc = bacc.Bacc("TRN2", target_bir_lowering=False, num_devices=1)
    arrays, A = {}, {}
    for name, v in _layout(inputs).items():
        a = np.ascontiguousarray(v)
        arrays[f"in_{name}"] = a
        A[name] = nc.dram_tensor(f"in_{name}", a.shape, mybir.dt.from_np(a.dtype), kind="ExternalInput").ap()
    out = nc.dram_tensor("out_x", (128, KT, LAT), mybir.dt.float32, kind="ExternalOutput").ap()
    program(nc, A, out)
    r = run_bass_kernel_spmd(nc, [arrays], core_ids=[0])
    y = r.results[0]["out_x"]
    return np.ascontiguousarray(y.transpose(2, 1, 0).reshape(1, LAT, D))
```
